# Optimizing a Trainium2 kernel written in Bass

```python
import jax, jax.numpy as jnp
from jax import lax
import numpy as np

D_MODEL = 1024
BATCH = 1
SEQ = 1024
DEPTH = 1
DEC_BATCH = 8
DEC_SEQ = 8
PAST_LEN = 1024
PAGE_SIZE = 128

HEAD_DIM = 64
HEADS_PER_GROUP = 4
GROUPS = ((128, 1), (512, 4), (2048, 16))
N_GROUPS = 3
N_ATT_HEADS = N_GROUPS * HEADS_PER_GROUP
ATT_W = N_ATT_HEADS * HEAD_DIM
ATT_OUT_W = HEADS_PER_GROUP * HEAD_DIM
CONV_W = D_MODEL // 2
CONV_K = 3
D_FF = 4 * D_MODEL
N_BUCKETS = 32
MAX_DISTANCE = 2048
BLOCK = 128
EPS = 1e-6
SCALE = HEAD_DIM ** -0.5
SPLITS = (ATT_W, ATT_W, ATT_W, CONV_W, CONV_W, CONV_W, D_MODEL, D_MODEL)
PROJ_W = 3 * ATT_W + 3 * CONV_W + 2 * D_MODEL

kernel_name = "hybrid_dilated_attn_gated_conv_step"

def rmsnorm(x, g):
    xf = x.astype(jnp.float32)
    y = xf * lax.rsqrt(jnp.mean(xf * xf, axis=-1, keepdims=True) + EPS)
    return (y * g.astype(jnp.float32)).astype(x.dtype)

def t5_bucket(dist):
    n = np.asarray(dist)
    max_exact = N_BUCKETS // 2
    large = max_exact + (np.log(np.maximum(n, 1) / max_exact) / np.log(MAX_DISTANCE / max_exact)
                         * (N_BUCKETS - max_exact)).astype(np.int32)
    large = np.minimum(large, N_BUCKETS - 1)
    return np.where(n < max_exact, n, large).astype(np.int32)

def group_bias(rel_bias, g):
    win, dil = GROUPS[g]
    kb = win // dil
    buckets = t5_bucket(np.arange(kb + 1) * dil)
    sl = slice(g * HEADS_PER_GROUP, (g + 1) * HEADS_PER_GROUP)
    return rel_bias[buckets][:, sl].astype(jnp.float32)

def dilated_attn_prompt(q, k, v, bias, dil, kb):
    B, S, H, E = q.shape
    L = S // dil
    nb = -(-L // BLOCK)
    Lp = nb * BLOCK

    def to_res(t):
        t = t.reshape(B, L, dil, H, E).transpose(0, 2, 1, 3, 4).astype(jnp.float32)
        return jnp.pad(t, ((0, 0), (0, 0), (0, Lp - L), (0, 0), (0, 0)))

    def windows(t):
        t = jnp.pad(to_res(t), ((0, 0), (0, 0), (BLOCK, 0), (0, 0), (0, 0)))
        t = t.reshape(B, dil, nb + 1, BLOCK, H, E)
        return jnp.concatenate([t[:, :, :-1], t[:, :, 1:]], axis=3)

    qb = to_res(q).reshape(B, dil, nb, BLOCK, H, E)
    kw, vw = windows(k), windows(v)
    a = np.arange(BLOCK)[:, None]
    c = np.arange(2 * BLOCK)[None, :]
    rel = BLOCK + a - c
    kidx = (np.arange(nb)[:, None, None] - 1) * BLOCK + c[None]
    valid = (rel >= 0) & (rel <= kb) & (kidx >= 0)
    bias_rel = bias[np.clip(rel, 0, kb)].transpose(2, 0, 1)
    s = jnp.einsum('bdnqhe,bdnkhe->bdnhqk', qb, kw) * SCALE + bias_rel[None, None, None]
    s = jnp.where(valid[None, None, :, None], s, -jnp.inf)
    lse = jax.nn.logsumexp(s, axis=-1)
    p = jnp.exp(s - lse[..., None])
    o = jnp.einsum('bdnhqk,bdnkhe->bdnqhe', p, vw)
    o = o.reshape(B, dil, Lp, H, E)[:, :, :L].transpose(0, 2, 1, 3, 4).reshape(B, S, H, E)
    lse = lse.transpose(0, 1, 2, 4, 3).reshape(B, dil, Lp, H)[:, :, :L]
    lse = lse.transpose(0, 2, 1, 3).reshape(B, S, H)
    return o, lse

def dilated_attn_sample(q, k, v, kv_buf, bias, dil, kb):
    Bd, T, H, E = q.shape
    Wb = kv_buf.shape[1]
    k_all = jnp.concatenate([kv_buf[:, :, 0].astype(k.dtype), k], axis=1).astype(jnp.float32)
    v_all = jnp.concatenate([kv_buf[:, :, 1].astype(v.dtype), v], axis=1).astype(jnp.float32)
    idx = Wb + np.arange(T)[:, None] - np.arange(kb + 1)[None, :] * dil
    valid = idx >= 0
    idx = np.maximum(idx, 0)
    kg = k_all[:, idx]
    vg = v_all[:, idx]
    s = jnp.einsum('bthe,btjhe->bhtj', q.astype(jnp.float32), kg) * SCALE + bias.T[None, :, None, :]
    s = jnp.where(valid[None, None], s, -jnp.inf)
    lse = jax.nn.logsumexp(s, axis=-1)
    p = jnp.exp(s - lse[..., None])
    o = jnp.einsum('bhtj,btjhe->bthe', p, vg)
    return o, lse.transpose(0, 2, 1)

def dilated_attention(q, k, v, rel_bias, kv_bufs):
    S = q.shape[1]
    outs, lses, rows = [], [], []
    for g, (win, dil) in enumerate(GROUPS):
        sl = slice(g * HEADS_PER_GROUP, (g + 1) * HEADS_PER_GROUP)
        kb = win // dil
        qg, kg, vg = q[:, :, sl], k[:, :, sl], v[:, :, sl]
        bias = group_bias(rel_bias, g)
        kv = jnp.stack([kg, vg], axis=2)
        if kv_bufs is None:
            o, l = dilated_attn_prompt(qg, kg, vg, bias, dil, kb)
            rows.append(kv[:, -min(win, S):])
        else:
            o, l = dilated_attn_sample(qg, kg, vg, kv_bufs[g], bias, dil, kb)
            rows.append(kv)
        outs.append(o)
        lses.append(l)
    w = jax.nn.softmax(jnp.stack(lses, 0), axis=0)
    o = jnp.einsum('gbsh,gbshe->bshe', w, jnp.stack(outs, 0))
    B = q.shape[0]
    return o.reshape(B, S, ATT_OUT_W), rows

def layer(x, conv_prefix, kv_bufs, rel_bias, w_in, w_att_out, w_conv_out, w_o, conv_w, conv_b,
          norm_mix, norm_mlp, w_ff1, w_ff2):
    B, S, _ = x.shape
    xn = rmsnorm(x, norm_mix)
    proj = xn @ w_in
    q, k, v, cb, cc, ch, ga, gb = jnp.split(proj, [int(i) for i in np.cumsum(SPLITS)[:-1]], axis=-1)
    q = q.reshape(B, S, N_ATT_HEADS, HEAD_DIM)
    k = k.reshape(B, S, N_ATT_HEADS, HEAD_DIM)
    v = v.reshape(B, S, N_ATT_HEADS, HEAD_DIM)
    att, kv_rows = dilated_attention(q, k, v, rel_bias, kv_bufs)
    u = cc * ch
    u_pad = jnp.concatenate([conv_prefix.astype(u.dtype), u], axis=1)
    z = conv_b + conv_w[0] * u_pad[:, 0:S] + conv_w[1] * u_pad[:, 1:S + 1] + conv_w[2] * u_pad[:, 2:S + 2]
    conv_state = u_pad[:, -(CONV_K - 1):]
    branch_a = att.astype(x.dtype) @ w_att_out
    branch_b = (cb * z) @ w_conv_out
    m = jax.nn.sigmoid(ga) * branch_a + jax.nn.sigmoid(gb) * branch_b
    x = x + m @ w_o
    h = rmsnorm(x, norm_mlp)
    x = x + jnp.square(jax.nn.relu(h @ w_ff1)) @ w_ff2
    return x, kv_rows, conv_state

def setup_inputs(seed: int = 0) -> dict:
    key = jax.random.key(seed)
    ks = jax.random.split(key, 20)
    f32 = jnp.float32
    n = lambda k, shape, s: jax.random.normal(k, shape, f32) * s
    wb = [min(win, PAST_LEN) for win, _ in GROUPS]
    return {
        "x_prompt": n(ks[0], (BATCH, SEQ, D_MODEL), 1.0),
        "x_sample": n(ks[1], (DEC_BATCH, DEC_SEQ, D_MODEL), 1.0),
        "cache_kv_g0": n(ks[2], (DEPTH, DEC_BATCH, wb[0], 2, HEADS_PER_GROUP, HEAD_DIM), 1.0),
        "cache_kv_g1": n(ks[3], (DEPTH, DEC_BATCH, wb[1], 2, HEADS_PER_GROUP, HEAD_DIM), 1.0),
        "cache_kv_g2": n(ks[4], (DEPTH, DEC_BATCH, wb[2], 2, HEADS_PER_GROUP, HEAD_DIM), 1.0),
        "state_conv": n(ks[5], (DEPTH, DEC_BATCH, CONV_K - 1, CONV_W), 1.0),
        "w_in": n(ks[6], (DEPTH, D_MODEL, PROJ_W), D_MODEL ** -0.5),
        "w_att_out": n(ks[7], (DEPTH, ATT_OUT_W, D_MODEL), ATT_OUT_W ** -0.5),
        "w_conv_out": n(ks[8], (DEPTH, CONV_W, D_MODEL), CONV_W ** -0.5),
        "w_o": n(ks[9], (DEPTH, D_MODEL, D_MODEL), D_MODEL ** -0.5),
        "conv_w": n(ks[10], (DEPTH, CONV_K, CONV_W), CONV_K ** -0.5),
        "conv_b": n(ks[11], (DEPTH, CONV_W), 0.02),
        "rel_bias": n(ks[12], (N_BUCKETS, N_ATT_HEADS), 0.5),
        "norm_mix": 1.0 + n(ks[13], (DEPTH, D_MODEL), 0.05),
        "norm_mlp": 1.0 + n(ks[14], (DEPTH, D_MODEL), 0.05),
        "w_ff1": n(ks[15], (DEPTH, D_MODEL, D_FF), D_MODEL ** -0.5),
        "w_ff2": n(ks[16], (DEPTH, D_FF, D_MODEL), D_FF ** -0.5),
        "norm_final": 1.0 + n(ks[17], (D_MODEL,), 0.05),
    }

def reference(x_prompt, x_sample, cache_kv_g0, cache_kv_g1, cache_kv_g2, state_conv, w_in, w_att_out,
              w_conv_out, w_o, conv_w, conv_b, rel_bias, norm_mix, norm_mlp, w_ff1, w_ff2, norm_final):
    caches = (cache_kv_g0, cache_kv_g1, cache_kv_g2)
    xp, xs = x_prompt, x_sample
    kvp = [[] for _ in range(N_GROUPS)]
    kvs = [[] for _ in range(N_GROUPS)]
    convp, convs = [], []
    for l in range(DEPTH):
        wts = (w_in[l], w_att_out[l], w_conv_out[l], w_o[l], conv_w[l], conv_b[l],
               norm_mix[l], norm_mlp[l], w_ff1[l], w_ff2[l])
        prompt_prefix = jnp.zeros((xp.shape[0], CONV_K - 1, CONV_W), xp.dtype)
        xp, rows_p, cp = layer(xp, prompt_prefix, None, rel_bias, *wts)
        xs, rows_s, cs = layer(xs, state_conv[l], [c[l] for c in caches], rel_bias, *wts)
        for g in range(N_GROUPS):
            kvp[g].append(rows_p[g])
            kvs[g].append(rows_s[g])
        convp.append(cp)
        convs.append(cs)
    y_prompt = rmsnorm(xp, norm_final)
    y_sample = rmsnorm(xs, norm_final)
    return (y_prompt, y_sample,
            jnp.stack(kvp[0], 0), jnp.stack(kvp[1], 0), jnp.stack(kvp[2], 0), jnp.stack(convp, 0),
            jnp.stack(kvs[0], 0), jnp.stack(kvs[1], 0), jnp.stack(kvs[2], 0), jnp.stack(convs, 0))


_drawn_inputs = setup_inputs


def setup_inputs(seed=0):
    import zlib

    import numpy as np

    out = dict(_drawn_inputs(seed))
    spreads = {}
    factors = {'conv_b': 5.296}
    for name, (base, spread) in spreads.items():
        noise = np.random.default_rng([zlib.crc32(name.encode()), seed]).standard_normal(out[name].shape)
        drawn = base * np.exp(spread * noise) if base else spread * noise
        out[name] = __import__('jax').numpy.asarray(drawn.astype(out[name].dtype))
    for name, factor in factors.items():
        out[name] = (out[name] * factor).astype(out[name].dtype)
    return out
```

```python
from contextlib import ExitStack

import numpy as np

import concourse.bass as bass
from concourse import mybir

F32 = mybir.dt.float32
F32R = mybir.dt.float32r
ACT = mybir.ActivationFunctionType
ALU = mybir.AluOpType
AX_X = mybir.AxisListType.X
ds = bass.ds

P = 128
D = 1024
KD = D // P
SEQ = 1024
NB_S, T_S = 8, 8
SAMP = NB_S * T_S
TOK = SEQ + SAMP
TILES = 9
GROUPS = ((128, 1), (512, 4), (2048, 16))
NG, NH, HD = 3, 4, 64
ATT_W = NG * NH * HD
GW = NH * HD
CONV_W = 512
FC = CONV_W // P
D_FF = 4096
N_BUCKETS, MAX_DISTANCE = 32, 2048
EPS = 1e-6
SCALE = HD ** -0.5
NEG = -1e30
HUGE = 3e38
CH = ((0, 352), (352, 368), (720, 368))
TABLE = 384
DIAG0 = 255

COL_Q, COL_B, COL_C, COL_H, COL_GA, COL_GB = 0, 2304, 2816, 3328, 3840, 4864
PROJ_W = 5888
S_QKV, S_PROMPT, S_SAMPLE, S_GATE, S_MIX, S_OUT, S_MLP, S_END = 0, 18, 30, 46, 54, 62, 70, 134


def bucket(dist):
    n = np.asarray(dist)
    exact = N_BUCKETS // 2
    large = exact + (np.log(np.maximum(n, 1) / exact) / np.log(MAX_DISTANCE / exact)
                     * (N_BUCKETS - exact)).astype(np.int32)
    return np.where(n < exact, n, np.minimum(large, N_BUCKETS - 1))


def bias_selector():
    sel = np.zeros((N_BUCKETS + 1, NG, TABLE), np.float32)
    for g, (win, dil) in enumerate(GROUPS):
        for w in range(TABLE):
            rel = DIAG0 - w
            if 0 <= rel <= win // dil:
                sel[bucket(rel * dil), g, w] = 1.0
            else:
                sel[N_BUCKETS, g, w] = NEG
    return sel.reshape(N_BUCKETS + 1, NG * TABLE)


def blocks(g):
    return [(g == 0 and i > 0) or (g == 1 and i % 2 == 1) for i in range(8)]


def key_products(g, half):
    lo, hi = 4 * half, 4 * half + 4
    out = []
    prev = blocks(g)
    if half and prev[lo]:
        out.append((lo - 1, lo, 1))
    for n in range(lo, hi):
        wide = n + 1 < hi and prev[n + 1]
        out.append((n, n, 2 if wide else 1))
    return out


class Step:

    def __init__(self, c, *terms):
        self.c, self.terms, self.p = c, terms, c % 2
        self.s, self.before = c, c // 2
        for factor, reg in terms:
            self.s = reg * factor + self.s
            self.before = reg * (factor // 2) + self.before

    def __add__(self, n):
        return Step(self.c + n, *self.terms)


def flat(ap):
    return ap.rearrange("p o t -> p (o t)")


def above_zero(value):
    return not isinstance(value, int) or value > 0


def wait_apart(eng, tab_in, *waits):
    values = [v if isinstance(v, int) else eng.compute_val(v) for _, v in waits]
    eng.wait_ge(tab_in, 16 * 7)
    for (sem, _), value in zip(waits, values):
        if above_zero(value):
            eng.wait_ge(sem, value)


def build(nc, x_p, x_s, ckv, state, w_in, w_att, w_conv, w_o, conv_w, conv_b, rel_bias, g_mix,
          g_mlp, w_ff1, w_ff2, g_fin, selector, identity, y_p, y_s, kvp, conv_p, kvs, conv_s):
    es = ExitStack()
    base = 16640
    at = lambda name, shape, off, dt=F32: nc.alloc_sbuf_tensor_at(name, list(shape), dt, offset=base + off)

    RA, RB, RC, RW, RD = 0, 69632, 139264, 174080, 198656

    xhi = at("xhi", [P, KD, TOK], RA, F32R)
    xlo = at("xlo", [P, KD, TOK], RA + 34816, F32R)
    mhi = at("mhi", [P, KD, TOK], RA, F32R)
    mlo = at("mlo", [P, KD, TOK], RA + 34816, F32R)
    fhi = at("fhi", [P, KD, TOK], RA, F32R)
    flo = at("flo", [P, KD, TOK], RA + 34816, F32R)
    wr = [at(f"wr{p}", [P, KD, P], RW + 4096 * p) for p in range(2)]
    wh = [at(f"wh{p}", [P, KD, P], RW + 8192 + 4096 * p, F32R) for p in range(2)]
    wl = [at(f"wl{p}", [P, KD, P], RW + 16384 + 4096 * p, F32R) for p in range(2)]
    onehot = at("onehot", [N_BUCKETS + 1, NG * TABLE], RC)
    btab = at("btab", [12, NG * TABLE], RC + 4608)
    relb = at("relb", [N_BUCKETS + 1, 12], RC + 9216)
    rows = at("rows", [20, CONV_W], RC + 9280)
    grow = at("grow", [KD, P], RC + 11328)
    toe2 = at("toe2", [P, NH, P], RC + 11840)
    bhi = at("bhi", [P, FC, TOK], RC, F32R)
    blo = at("blo", [P, FC, TOK], RC + 17408, F32R)
    x2 = at("x2", [P, KD, TOK], RC)
    ident = at("ident", [P, P], RD)
    cT = at("cT", [P, FC * 20], RD + 512)
    g2c = at("g2c", [P, KD], RD + 832)
    ssq = at("ssq", [P, 16], RD + 864)
    rst = at("rst", [P, 5, 16], RD + 928)
    st = [at(f"st{p}", [P, 16], RD + 1248 + 64 * p) for p in range(2)]
    stT = [at(f"stT{p}", [16, P], RD + 1376 + 512 * p) for p in range(2)]
    us = at("us", [P, NB_S, T_S + 2], RD + 2400)
    csb = at("csb", [P, FC, 18], RD + 2720)
    bias_s = at("bias_s", [32, 1176], RD + 3008)
    cst = at("cst", [18, CONV_W], RD + 7712)
    cO = at("cO", [P, 2, NG, P], RD + 7712)
    cC = at("cC", [P, 2, NG, P], RD + 10784)
    sm = at("sm", [32, 16], RD + 13856)
    ones = at("ones", [P, P], RD + 7712)
    ssqa = at("ssqa", [P, TOK], RD + 8224)
    sq2 = at("sq2", [P, TOK], RD + 3008)
    r2b = at("r2b", [P, TOK], RD + 3008)
    xt = at("xt", [P, TILES, D], RB)
    gb = at("gb", [P, D], RB + 36864)
    junk = at("junk", [P, D], RB + 40960)
    stg = [at(f"stg{p}", [P, TOK], RB + 45056 + 4352 * p) for p in range(2)]
    tm = [at(f"tm{p}", [P, TILES, P], RB + 53760 + 4608 * p) for p in range(2)]
    qT = [at(f"qT{p}", [HD, SEQ], RB + 4096 * p) for p in range(2)]
    kT = [at(f"kT{p}", [HD, SEQ], RB + 8192 + 4096 * p) for p in range(2)]
    vU = [at(f"vU{p}", [P, 8, HD], RB + 16384 + 2048 * p) for p in range(2)]
    bU = [at(f"bU{p}", [P, 2 * P], RB + 20480 + 1024 * p) for p in range(2)]
    pS = at("pS", [P, 8, 2 * P], RB + 22528)
    pT = at("pT", [P, 16 * P], RB + 30720)
    oS = [at(f"oS{p}", [HD, SEQ], RB + 38912 + 4096 * p) for p in range(2)]
    U = at("U", [P, FC, TOK], RB + 47104)
    z = at("z", [P, TOK], RB + 64512)
    kvc = at("kvc", [P, TILES, 2 * GW], RB)
    kTs = at("kTs", [P, 2, TILES * P], RB + 18432)
    cf = at("cf", [32, 18, P], RB + 52224)
    xs = at("xs", [32, 1176], RB + 27648)
    pTs = at("pTs", [P, 320], RB + 32384)
    qbd = at("qbd", [P, 6, 32], RB + 33664)
    kst = at("kst", [P, 6, T_S], RB + 34432)
    vn = at("vn", [NG * T_S, GW], RB + 34624)
    osn = at("osn", [32, GW], RB + 35648)
    sg = at("sg", [P, TOK], RB + 36864)
    ats = at("ats", [P, 2, SAMP], RB + 41216)
    cS = at("cS", [P, 2, P], RB + 41728)
    bb = at("bb", [P, TOK], RB + 47104)
    athi = at("athi", [P, 2, TOK], RB + 52224, F32R)
    atlo = at("atlo", [P, 2, TOK], RB + 60928, F32R)
    xp = [at(f"xp{p}", [P, TILES, P], RB + 8192 + 4608 * p) for p in range(2)]
    sga = at("sga", [P, KD, TOK], RB + 17408)
    ml = [at(f"ml{p}", [P, TOK], RB + 4352 * p) for p in range(2)]
    mt = [at(f"mt{p}", [P, TOK], RB + 8704 + 4352 * p) for p in range(2)]
    hhi = at("hhi", [P, KD, TOK], RB, F32R)
    hlo = at("hlo", [P, KD, TOK], RB + 34816, F32R)
    rel = [at(f"rel{i}", [P, 368], RD + 7712 + 1472 * i) for i in range(2)]
    acc = at("acc", [P, 368], RD + 7712 + 2944)
    gf = at("gf", [P, D], RB)
    yt = [at(f"yt{p}", [P, D], RB + 4096 + 4096 * p) for p in range(3)]
    yj = at("yj", [P, 2, 512], RB + 16384)

    bank = [es.enter_context(nc.psum_tensor(f"bank{i}", [P, 512], F32)) for i in range(8)]

    scratch = lambda name, shape: nc.dram_tensor(name, shape, F32, kind="Internal").ap()
    d_T = scratch("d_T", [3, ATT_W, TOK])
    d_tm = scratch("d_tm", [2, NG, TILES, P, GW])
    d_bt = scratch("d_bt", [12, NG, TABLE])
    d_skew = scratch("d_skew", [12, P * TABLE])
    d_toe2 = scratch("d_toe2", [NH, P, P])
    d_O = scratch("d_O", [NG * NH, HD, SEQ])
    d_st = scratch("d_st", [NG * NH, 16, P])
    d_c = scratch("d_c", [NG, NH, 8, P])
    d_m = scratch("d_m", [KD, P, TOK])


    def sem(name):
        return es.enter_context(nc.semaphore(name))

    w_raw = [sem("weights_in0"), sem("weights_in1")]
    w_hi, w_lo, ready = sem("weights_hi"), sem("weights_lo"), sem("chunk_ready")
    taken = [sem(f"chunk{c}_taken") for c in range(3)]
    tab_in, gb_in, x_in = sem("tables_in"), sem("g_mix_in"), [sem(f"x_in{t}") for t in range(TILES)]
    relb_one, ssq_one, toe_neg, sbias_neg = sem("mask_row_set"), sem("ssq_set"), sem("toeplitz_masked"), sem("sample_bias_masked")
    bt_pe, bt_a, bt_st, const_d = sem("table_multiplied"), sem("table_copied"), sem("table_stored"), sem("constants_copied")
    toe_in, toe_st, sb_in = sem("toeplitz_in"), sem("toeplitz_stored"), sem("sample_bias_in")
    x_sq, rs_d, rs_a = sem("x_squares"), sem("rstd_by_dve"), sem("rstd_root")
    x_scaled, x_pe, x_hi, x_lo = sem("x_scaled"), sem("x_turned"), sem("x_hi"), sem("x_lo")
    stg_a = sem("stage_prompt_tail")
    stg_st = [sem("stage_stored0"), sem("stage_stored1")]
    tm_pe, tm_a, tm_d = sem("token_major_turned"), sem("token_major_by_act"), sem("token_major_by_dve")
    tm_st = [sem("token_major_stored0"), sem("token_major_stored1")]
    u_in = [sem("unit_in0"), sem("unit_in1")]
    s_pe, s_d, s_a = sem("scores"), sem("scores_biased"), sem("scores_exp")
    pt_pe, pt_a, pt_d = sem("probs_turned"), sem("probs_by_act"), sem("probs_by_dve")
    pv_pe, o_a, o_d = sem("values"), sem("out_by_act"), sem("out_by_dve")
    o_st = [sem("out_stored0"), sem("out_stored1")]
    cs_d, cs_pe, cs_ev, cs_st = sem("state_gathered"), sem("state_turned"), sem("state_copied"), sem("state_stored")
    z_d, b_hi, b_lo = sem("z_terms"), sem("b_hi"), sem("b_lo")
    cf_in, cf_d, cf_a, cf_st = sem("stats_in"), sem("coef_by_dve"), sem("coef_exp"), sem("coef_stored")
    q_zero, k_in, v_in = sem("q_zeroed"), sem("sample_keys_in"), sem("sample_values_in")
    kt_pe, kt_a, kt_d = sem("keys_turned"), sem("keys_by_act"), sem("keys_by_dve")
    xq_pe, xq_d, xq_a, rl_d = sem("sample_scores"), sem("sample_biased"), sem("sample_exp"), sem("sample_sums")
    sv_pe, sn_d, so_pe, ats_a = sem("sample_values"), sem("sample_normed"), sem("sample_out_turned"), sem("sample_out")
    mb_d, m_st = sem("gated_convolution"), sem("gates_stored")
    cm_in, cm_d, at_hi, at_lo = sem("combine_in"), sem("combined"), sem("att_hi"), sem("att_lo")
    res_in, mix_in = [sem("residual_in0"), sem("residual_in1")], [sem("mix_in0"), sem("mix_in1")]
    res_pe, res_d = sem("residual_turned"), sem("residual_copied")
    mt_p, m_hi, m_lo = sem("mixed"), sem("m_hi"), sem("m_lo")
    sq_a, sqa_p, h_hi, h_lo = sem("x2_squares"), sem("squares_added"), sem("h_hi"), sem("h_lo")
    ones_p, n2_pe, r2_d = sem("ones_set"), sem("norm2_sum"), sem("norm2")
    f_rel, f_hi, f_lo, y_d = sem("relu"), sem("f_hi"), sem("f_lo"), sem("mlp_added")
    gf_in, yt_pe, yt_a, yn_d, yr_a, yt_d = (sem("g_final_in"), sem("y_turned"), sem("y_squares"), sem("y_rstd"),
                                            sem("y_root"), sem("y_normed"))
    y_st = [sem(f"y_stored{i}") for i in range(3)]

    block = es.enter_context(nc.Block())

    view = lambda w: w.rearrange("(k p) c -> p k c", p=P)
    W_IN, W_CONV, W_ATT, W_O, W_1 = (view(w) for w in (w_in, w_conv, w_att, w_o, w_ff1))
    W_2 = w_ff2.rearrange("(q k p) c -> q p k c", q=4, p=P)
    xs_dram = x_s.rearrange("b t d -> (b t) d")
    rows_of = lambda t: P if t < 8 else SAMP
    prompt_col = {0: COL_C, 1: COL_H, 2: COL_B}

    TM_STORES = (4, 4, 5)

    def tm_total(par):
        return 16 * sum(TM_STORES[k // 2] for k in range(par, 6, 2))

    def tm_before(k, i):
        return i * tm_total(k % 2) + 16 * sum(TM_STORES[j // 2] for j in range(k % 2, k, 2))

    def col(ap, h, n, lo, hi):
        return ap[:, h, lo:hi] if isinstance(h, int) else flat(ap[:, ds(h, 1), lo:hi])

    def stage_chunk(p, g, c):
        t0, n = CH[c]
        n = min(n, SEQ - t0)
        dil = GROUPS[g][1]
        if dil == 1:
            return stg[p][:, t0:t0 + n], bank[c][:, 0:n]
        return (stg[p][:, 0:SEQ].rearrange("p (r m) -> p m r", r=dil)[:, t0 // dil:(t0 + n) // dil, :],
                bank[c][:, 0:n].rearrange("p (m r) -> p m r", r=dil))

    def probs_copy(g, j, src):
        prev = blocks(g)
        if not prev[2 * j + 1]:
            v = lambda ap: ap.rearrange("p (i k c) -> p i k c", i=2, k=2)[:, :, 1, :]
            return v(pT[:, 512 * j:512 * j + 512]), v(src[:])
        lo = 0 if prev[2 * j] else P
        return pT[:, 512 * j + lo:512 * j + 512], src[:, lo:512]

    def out_copy(g, p, half):
        dil = GROUPS[g][1]
        src = bank[5][0:HD, :]
        if dil == 1:
            return oS[p][:, 512 * half:512 * half + 512], src
        n = dil // 2
        return (oS[p][:].rearrange("p (m r) -> p m r", r=dil)[:, :, n * half:n * half + n],
                src.rearrange("p (r m) -> p m r", r=n))

    @block.sync
    def _(sp):
        def weights(src, nk, st_):
            if above_zero(st_.s - 1):
                sp.wait_ge(w_lo, st_.s - 1)
            sp.dma_start(wr[st_.p][:, 0:nk, :], src).then_inc(w_raw[st_.p], 16)

        for t in range(TILES):
            if t < 8:
                sp.dma_start(xt[:, t, :], x_p[0, t * P:(t + 1) * P, :]).then_inc(x_in[t], 16)
            else:
                sp.dma_start(xt[0:SAMP, 8, :], xs_dram).then_inc(x_in[t], 16)
            if t == 0:
                sp.dma_start(ident[:], identity).then_inc(tab_in, 16)
                sp.dma_start(onehot[:], selector).then_inc(tab_in, 16)
                sp.dma_start(relb[0:N_BUCKETS, :], rel_bias).then_inc(tab_in, 16)
                sp.dma_start(rows[0:16, :], state.rearrange("l b k c -> (l b k) c")).then_inc(tab_in, 16)
                sp.dma_start(rows[16:19, :], conv_w[0]).then_inc(tab_in, 16)
                sp.dma_start(rows[19:20, :], conv_b).then_inc(tab_in, 16)
                sp.dma_start(grow[:], g_mlp[0].rearrange("(k p) -> k p", p=P)).then_inc(tab_in, 16)
            if t == 4:
                sp.dma_start(gb[:], bass.AP(g_mix.tensor, 0, [[0, P], [1, D]])).then_inc(gb_in, 16)
        for k in range(2):
            weights(W_IN[:, :, k * P:(k + 1) * P], KD, Step(k))

        sp.wait_ge(bt_st, 16)
        table = lambda g, h: ((g * NH + h) * NG + g) * TABLE
        for g in range(NG):
            for h in range(NH):
                sp.dma_start(d_skew[g * NH + h].rearrange("(p c) -> p c", c=TABLE),
                             bass.AP(d_bt.tensor, table(g, h), [[0, P], [1, TABLE]])).then_inc(toe_st, 16)
        sp.wait_ge(toe_st, 16 * 12)
        sp.wait_ge(toe_neg, 1)
        for h in range(NH):
            for r in range(2):
                sp.dma_start(toe2[64 * r:64 * r + 64, h, 64 * r:64 * r + 64],
                             bass.AP(d_skew.tensor, (2 * NH + h) * P * TABLE + DIAG0, [[TABLE - 1, 64], [1, 64]])).then_inc(toe_in, 16)
        sp.wait_ge(toe_in, 16 * 8)
        sp.dma_start(d_toe2.rearrange("h p c -> p h c"), toe2[:]).then_inc(toe_st, 16)
        sp.wait_ge(sbias_neg, 1)
        rowh = NG * TABLE
        sp.dma_start(bias_s[:, 0:136], bass.AP(d_skew.tensor, P - 1, [[P * TABLE, NH], [TABLE - 1, T_S], [1, 136]])).then_inc(sb_in, 16)
        with nc.allow_non_contiguous_dma(reason="a few single biases"):
            for t in range(T_S):
                r, q = t % 4, t // 4
                part = bias_s[t:32:T_S, :]
                sp.dma_start(part[:, 152 + P * r:152 + P * r + P],
                             bass.AP(d_bt.tensor, table(1, 0) + 127 - q, [[rowh, NH], [1, P]])).then_inc(sb_in, 16)
                sp.dma_start(part[:, 136 + r:144:4],
                             bass.AP(d_bt.tensor, table(1, 0) + DIAG0 - q, [[rowh, NH], [1, 2]])).then_inc(sb_in, 16)
                sp.dma_start(part[:, 664 + P * r + 64 * q:664 + P * r + 64 * q + 64],
                             bass.AP(d_bt.tensor, table(2, 0) + 191, [[rowh, NH], [1, 64]])).then_inc(sb_in, 16)
                sp.dma_start(part[:, 144 + t:145 + t],
                             bass.AP(d_bt.tensor, table(2, 0) + DIAG0, [[rowh, NH], [1, 1]])).then_inc(sb_in, 16)

        for k in range(2, 6):
            weights(W_IN[:, :, k * P:(k + 1) * P], KD, Step(k))
        with sp.Fori(0, 2) as i:
            for k in range(6):
                weights(W_IN[:, :, ds(i * ATT_W + (ATT_W + k * P), P)], KD, Step(6 + k, (6, i)))

        def unit_weights(g, i, p):
            weights(W_IN[:, :, ds(i * (2 * P) + (prompt_col[g] + p * P), P)], KD, Step(S_PROMPT + 4 * g + p, (2, i)))

        for p in range(2):
            sp.wait_ge(stg_st[p], 16 * 4)
            sp.wait_ge(tm_st[p], tm_total(p) + 16 * TM_STORES[0])
        sp.wait_ge(toe_st, 16 * 13)

        def unit(g, i, p):
            h = i * 2 + p
            if above_zero(i * 4 + (8 * g + 2 * p - 2)):
                sp.wait_ge(pv_pe, i * 4 + (8 * g + 2 * p - 2))
            rows_ = ds(i * (2 * HD) + (g * GW + p * HD), HD)
            sp.dma_start(qT[p][:], d_T[0, rows_, 0:SEQ]).then_inc(u_in[p], 16)
            sp.dma_start(kT[p][:], d_T[1, rows_, 0:SEQ]).then_inc(u_in[p], 16)
            sp.dma_start(vU[p][:], d_tm[1, g, 0:8, :, ds(i * (2 * HD) + p * HD, HD)].rearrange("i p e -> p i e")).then_inc(u_in[p], 16)
            if g == 2:
                sp.dma_start(bU[p][:, P:2 * P], d_toe2[ds(h, 1)].rearrange("h p c -> (h p) c")).then_inc(u_in[p], 16)
            else:
                skewed = d_skew[ds(i * 2 + (NH * g + p), 1), P - 1:P - 1 + (TABLE - 1) * P]
                sp.dma_start(bU[p][:], skewed.rearrange("h (p c) -> (h p) c", c=TABLE - 1)[:, 0:2 * P]).then_inc(u_in[p], 16)

        for p in range(2):
            unit(0, 0, p)
        for p in range(2):
            unit_weights(0, 0, p)
        for p in range(2):
            sp.wait_ge(stg_st[p], 16 * 9)
            sp.wait_ge(tm_st[p], 2 * tm_total(p))
        for p in range(2):
            unit_weights(0, 1, p)
            unit(0, 1, p)
        for g in (1, 2):
            with sp.Fori(0, 2) as i:
                for p in range(2):
                    unit_weights(g, i, p)
                    unit(g, i, p)

        def conv_weights(b):
            weights(W_CONV[:, :, ds(b * P, P)], FC, Step(S_SAMPLE, (2, b)))

        def gate_b_weights(b):
            weights(W_IN[:, :, ds(b * P + COL_GB, P)], KD, Step(S_SAMPLE + 1, (2, b)))

        def key_loads(b):
            sp.dma_start(kvc[:, 0, 0:GW], ckv[0][0, ds(b, 1), :, 0].rearrange("b m h e -> (b m) (h e)")).then_inc(k_in, 16)
            sp.dma_start(kvc[:, 1:5, 0:GW], ckv[1][0, ds(b, 1), :, 0].rearrange("b (m r) h e -> (b m) r (h e)", r=4)).then_inc(k_in, 16)
            far = ckv[2][0, ds(b, 1), :, 0].rearrange("b (m r) h e -> (b m) r (h e)", r=16)
            for q in range(2):
                sp.dma_start(kvc[64 * q:64 * q + 64, 5:9, 0:GW], far[:, 4 * q:4 * q + 4, :]).then_inc(k_in, 16)
            if isinstance(b, int):
                sp.wait_ge(q_zero, 1)
            for h in range(NH):
                half = 64 * (h % 2)
                sp.dma_start(qbd[half:half + 64, h // 2::2, h * T_S:(h + 1) * T_S],
                             d_T[0].rearrange("(g h e) t -> h e g t", g=NG, h=NH)[h, :, :, ds(b * T_S + SEQ, T_S)]).then_inc(k_in, 16)
            sp.dma_start(kst[:], d_T[1].rearrange("(j p) t -> p j t", p=P)[:, :, ds(b * T_S + SEQ, T_S)]).then_inc(k_in, 16)

        def value_loads(b):
            sp.dma_start(kvc[:, 0, GW:2 * GW], ckv[0][0, ds(b, 1), :, 1].rearrange("b m h e -> (b m) (h e)")).then_inc(v_in, 16)
            sp.dma_start(kvc[:, 1:5, GW:2 * GW], ckv[1][0, ds(b, 1), :, 1].rearrange("b (m r) h e -> (b m) r (h e)", r=4)).then_inc(v_in, 16)
            far = ckv[2][0, ds(b, 1), :, 1].rearrange("b (m r) h e -> (b m) r (h e)", r=16)
            for q in range(2):
                sp.dma_start(kvc[64 * q:64 * q + 64, 5:9, GW:2 * GW], far[:, 4 * q:4 * q + 4, :]).then_inc(v_in, 16)
            for g in range(NG):
                sp.dma_start(vn[g * T_S:(g + 1) * T_S, :], d_tm[1, g, 8, ds(b * T_S, T_S), :]).then_inc(v_in, 16)

        def combine_loads(n):
            for hp in range(2):
                sp.dma_start(cO[:, hp, :, :],
                             d_O.rearrange("(g q h) e t -> q (h e) g t", g=NG, q=2)[hp, :, :, ds(n * P, P)]).then_inc(cm_in, 16)
                for h2 in range(2):
                    sp.dma_start(cC[64 * h2:64 * h2 + 64, hp, :, :],
                                 bass.AP(d_c.tensor, n * P + (2 * hp + h2) * SEQ, [[0, 64], [NH * SEQ, NG], [1, P]])).then_inc(cm_in, 16)

        conv_weights(0)
        sp.wait_ge(s_pe, 48)
        sp.wait_ge(pv_pe, 22)
        key_loads(0)
        value_loads(0)
        gate_b_weights(0)
        sp.wait_ge(z_d, 28)
        for p in range(2):
            sp.wait_ge(o_st[p], 32 * 6)
        for k in range(2):
            for g in range(NG):
                stats = lambda h: ((g * NH + h) * 16 + 8 * k) * P
                dil = GROUPS[g][1]
                run = P // dil
                if g == 0:
                    sp.dma_start(cf[:, 3 * k, :], bass.AP(d_st.tensor, stats(0), [[16 * P, NH], [P, 8], [1, P]])).then_inc(cf_in, 16)
                else:
                    for h in range(NH):
                        sp.dma_start(cf[8 * h:8 * h + 8, 3 * k + g, :],
                                     bass.AP(d_st.tensor, stats(h), [[run, 8], [SEQ // dil, dil], [1, run]])).then_inc(cf_in, 16)
        sp.wait_ge(cs_st, 32)
        with sp.Fori(1, NB_S) as b:
            conv_weights(b)
            sp.wait_ge(kt_pe, b * 6 - 1)
            sp.wait_ge(xq_pe, b)
            key_loads(b)
            sp.wait_ge(cf_st, 48)
            wait_apart(sp, tab_in, (cm_d, b * 3 - 3))
            combine_loads(b - 1)
            gate_b_weights(b)
            sp.wait_ge(sv_pe, b)
            value_loads(b)

        def gate_a_weights(i, p):
            weights(W_IN[:, :, ds(i * (2 * P) + (COL_GA + p * P), P)], KD, Step(S_GATE + p, (2, i)))

        def residual_loads(i, p):
            if above_zero(i * 6 + 3 * (p - 1)):
                sp.wait_ge(res_pe, i * 6 + 3 * (p - 1))
            j = i * 2 + p
            sp.dma_start(xp[p][:, 0:8, :], x_p[0].rearrange("(t p) d -> p t d", p=P)[:, :, ds(j * P, P)]).then_inc(res_in[p], 16)
            sp.dma_start(xp[p][0:SAMP, 8, :], xs_dram[:, ds(j * P, P)]).then_inc(res_in[p], 16)

        gate_a_weights(0, 0)
        sp.wait_ge(cm_d, 21)
        combine_loads(NB_S - 1)
        gate_a_weights(0, 1)
        sp.wait_ge(sv_pe, NB_S)
        for p in range(2):
            residual_loads(0, p)
        with sp.Fori(1, 4) as i:
            for p in range(2):
                gate_a_weights(i, p)
                residual_loads(i, p)

        def mix_weights(i, p):
            weights(W_ATT[:, :, ds(i * (2 * P) + p * P, P)], 2, Step(S_MIX + p, (2, i)))

        def mix_loads(i, p):
            if above_zero(i * 2 + (p - 1)):
                sp.wait_ge(mt_p, i * 2 + (p - 1))
            sp.dma_start(ml[p][:], d_m[ds(i * 2 + p, 1)].rearrange("o p t -> (o p) t")).then_inc(mix_in[p], 16)

        for p in range(2):
            mix_weights(0, p)
        sp.wait_ge(m_st, 16 * NB_S)
        sp.wait_ge(res_pe, 24)
        for p in range(2):
            mix_loads(0, p)
        with sp.Fori(1, 4) as i:
            for p in range(2):
                mix_weights(i, p)
                mix_loads(i, p)
        with sp.Fori(0, 4) as i:
            for p in range(2):
                weights(W_O[:, :, ds(i * (2 * P) + p * P, P)], KD, Step(S_OUT + p, (2, i)))
        with sp.Fori(0, 4) as q:
            with sp.Fori(0, 4) as i:
                for p in range(2):
                    weights(W_1[:, :, ds(q * D + i * (2 * P) + p * P, P)], KD, Step(S_MLP + p, (16, q), (2, i)))
            with sp.Fori(0, 4) as i:
                for p in range(2):
                    weights(W_2[ds(q, 1)].rearrange("q p k c -> p (q k) c")[:, :, ds(i * (2 * P) + p * P, P)], KD,
                            Step(S_MLP + 8 + p, (16, q), (2, i)))

        sp.wait_ge(ready, 3 * S_END)
        sp.dma_start(gf[:], bass.AP(g_fin.tensor, 0, [[0, P], [1, D]])).then_inc(gf_in, 16)
        for t in range(TILES):
            sp.wait_ge(yt_d, 2 * (t + 1))
            if t < 8:
                sp.dma_start(y_p[0, t * P:(t + 1) * P, :], yt[t % 3][:]).then_inc(y_st[t % 3], 16)
            else:
                sp.dma_start(y_s.rearrange("b t d -> (b t) d"), yt[t % 3][0:SAMP, :]).then_inc(y_st[t % 3], 16)
        for t in range(3):
            sp.wait_ge(y_st[t], 48)

    @block.tensor
    def _(pe):
        def chunk(st_, nk, c, hi, lo, tile_wait=None):
            if c == 0:
                pe.wait_ge(w_lo, st_.s + 1)
            if above_zero(st_.s):
                pe.wait_ge(taken[c], st_.s)
            t0, n = CH[c]
            for k in range(nk):
                if tile_wait:
                    tile_wait(k)
                a, b = hi[:, k, t0:t0 + n], lo[:, k, t0:t0 + n]
                pe.matmul(bank[c][:, 0:n], wh[st_.p][:, k, :], a, start=(k == 0), stop=False)
                pe.matmul(bank[c][:, 0:n], wh[st_.p][:, k, :], b, start=False, stop=False)
                last = pe.matmul(bank[c][:, 0:n], wl[st_.p][:, k, :], a, start=False, stop=(k == nk - 1))
            last.then_inc(ready, 1)

        pe.wait_ge(tab_in, 16 * 7)
        pe.wait_ge(relb_one, 1)
        for g in range(NG):
            pe.matmul(bank[3 + g][0:12, 0:TABLE], relb[:], onehot[:, g * TABLE:(g + 1) * TABLE],
                      start=True, stop=True).then_inc(bt_pe, 1)
        for f in range(FC):
            pe.transpose(bank[6][:, 20 * f:20 * f + 20], rows[:, f * P:(f + 1) * P], ident[0:20, 0:20])
        pe.transpose(bank[6][:, 80:88], grow[:], ident[0:KD, 0:KD]).then_inc(bt_pe, 1)

        for t in range(TILES):
            w = rows_of(t)
            pe.wait_ge(x_scaled, t + 1)
            for half in range(2):
                n = 2 * t + half
                if n == 0:
                    pe.wait_ge(bt_a, 3)
                    pe.wait_ge(const_d, 2)
                if above_zero(n - 3):
                    pe.wait_ge(x_lo, n - 3)
                for k in range(4):
                    last = pe.transpose(bank[3 + n % 4][:, k * P:k * P + w],
                                        xt[0:w, t, (4 * half + k) * P:(4 * half + k + 1) * P], ident[0:w, 0:w])
                last.then_inc(x_pe, 1)

        def turn(kv, k, grp):
            if grp == 0:
                pe.wait_ge(stg_a, kv + 7)
                for c in range(3):
                    pe.wait_ge(taken[c], kv + 7)
                pe.wait_ge(x_lo, 2 * TILES)
            wait_apart(pe, tab_in, (tm_a if grp == 1 else tm_d, kv if grp == 1 else kv * 2))
            for i in range(4 * grp, min(4 * grp + 4, TILES)):
                w = rows_of(i)
                last = pe.transpose(bank[3 + grp][0:w, (i % 4) * P:(i % 4) * P + P], stg[k % 2][:, i * P:i * P + w], ident[:])
            last.then_inc(tm_pe, 1)

        for s in range(6):
            for c in range(3):
                if s == 0:
                    pe.wait_ge(x_lo, 2 * (3, 6, 9)[c])
                chunk(Step(s), KD, c, xhi, xlo)
        with pe.Fori(0, 2) as i:
            for k in range(6):
                for c in range(3):
                    chunk(Step(6 + k, (6, i)), KD, c, xhi, xlo)
                    if k:
                        turn(i * 6 + (k - 1), k - 1, c)
            for c in range(3):
                turn(i * 6 + 5, 5, c)

        def scores(g, i, p, j):
            if j == 0:
                pe.wait_ge(u_in[p], i * 64 + 64 * (2 * g + 1))
            pe.wait_ge(s_d, i * 16 + (32 * g + 8 * p + 2 * j - 2) if g or p or j else i * 16)
            for n in (2 * j, 2 * j + 1):
                prev = blocks(g)[n]
                c0 = (n % 2) * 256
                last = pe.matmul(bank[3 + j % 2][:, c0 + (0 if prev else P):c0 + 256], qT[p][:, n * P:(n + 1) * P],
                                 kT[p][:, (n - prev) * P:(n + 1) * P], start=True, stop=True)
            last.then_inc(s_pe, 1)

        RING = {0: (pt_d, 2, 0), 1: (pt_a, 3, 0), 2: (pt_a, 3, 1), 3: (pt_d, 2, 1), 4: (pt_a, 3, 2)}

        def ring_free(g, i, p, j):
            s_, per, n = RING[j]
            pe.wait_ge(s_, i * (2 * per) + (per * (4 * g + p) + n))

        def turn_probs(g, i, p, j):
            pe.wait_ge(s_a, i * 16 + (32 * g + 8 * p + 2 * j + 2))
            ring_free(g, i, p, j)
            out = bank[6 + (5 * p + j) % 2]
            for n in (2 * j, 2 * j + 1):
                c0 = (n % 2) * 256
                if blocks(g)[n]:
                    pe.transpose(out[:, c0:c0 + P], pS[:, n, 0:P], ident[:])
                last = pe.transpose(out[:, c0 + P:c0 + 256], pS[:, n, P:2 * P], ident[:])
            last.then_inc(pt_pe, 1)

        def values(g, i, p, half):
            u0 = 4 * g + p
            pe.wait_ge(pt_a, i * 6 + (3 * u0 + 1 + half))
            pe.wait_ge(pt_d, i * 4 + (2 * u0 + 1 + half))
            pe.wait_ge(o_d if half else o_a, i * 2 + (u0 + half))
            for n, (key, q0, nq) in enumerate(key_products(g, half)):
                c0 = (2 * key + 1) * P + (q0 - key) * P
                last = pe.matmul(bank[5][0:HD, (q0 - 4 * half) * P:(q0 - 4 * half + nq) * P], vU[p][:, key, :],
                                 pT[:, c0:c0 + nq * P], start=(n == 0), stop=True, skip_group_check=True)
            last.then_inc(pv_pe, 1)

        def turn_stats(g, i, p):
            ring_free(g, i, p, 4)
            pe.transpose(bank[6 + (5 * p + 4) % 2][0:16, 0:P], st[p][:], ident[:]).then_inc(pt_pe, 1)

        pe.wait_ge(tm_d, 24)
        pe.wait_ge(tm_a, 12)
        for g in range(NG):
            if g == 2:
                pe.wait_ge(cs_d, 2)
                pe.wait_ge(s_d, 64)
                for f in range(FC):
                    last = pe.transpose(bank[3][0:18, f * P:(f + 1) * P], csb[:, f, :], ident[:])
                last.then_inc(cs_pe, 1)
                pe.wait_ge(cs_ev, 1)
            with pe.Fori(0, 2) as i:
                for p in range(2):
                    st_ = Step(S_PROMPT + 4 * g + p, (2, i))
                    scores(g, i, p, 0)
                    scores(g, i, p, 1)
                    chunk(st_, KD, 0, xhi, xlo)
                    scores(g, i, p, 2)
                    scores(g, i, p, 3)
                    turn_probs(g, i, p, 0)
                    turn_probs(g, i, p, 1)
                    chunk(st_, KD, 1, xhi, xlo)
                    turn_probs(g, i, p, 2)
                    turn_probs(g, i, p, 3)
                    values(g, i, p, 0)
                    chunk(st_, KD, 2, xhi, xlo)
                    values(g, i, p, 1)
                    turn_stats(g, i, p)

        KEYS = [[(0, 1 + n) for n in range(4)], [(0, 5 + n) for n in range(4)],
                [(1, 1 + n) for n in range(4)], [(1, 5 + n) for n in range(4)], [(0, 0), (1, 0)]]

        def turn_keys(b, j):
            if j == 0:
                pe.wait_ge(k_in, b * 144 + 144)
            pe.wait_ge(kt_a if j % 2 == 0 else kt_d, b * (3 if j % 2 == 0 else 4) + j // 2)
            for n, (hp, tile) in enumerate(KEYS[j]):
                last = pe.transpose(bank[6 + j % 2][:, n * P:(n + 1) * P], kvc[:, tile, hp * P:(hp + 1) * P], ident[:])
            last.then_inc(kt_pe, 1)

        def sample_scores(b):
            pe.wait_ge(kt_a, b * 3 + 3)
            pe.wait_ge(kt_d, b * 4 + 2)
            pe.wait_ge(sn_d, b)
            pe.wait_ge(ats_a, b * 4)
            for hp in range(2):
                pe.matmul(bank[3][0:32, 0:P], qbd[:, hp, :], kTs[:, hp, 0:P], start=(hp == 0), stop=(hp == 1),
                          skip_group_check=True)
            for g in range(NG):
                for hp in range(2):
                    pe.matmul(bank[3][0:32, P + 8 * g:P + 8 * g + 8], qbd[:, 2 * g + hp, :], kst[:, 2 * g + hp, :],
                              start=False, stop=(hp == 1), skip_group_check=True)
            for g in (1, 2):
                for hp in range(2):
                    last = pe.matmul(bank[3 + g][0:32, :], qbd[:, 2 * g + hp, :], kTs[:, hp, P + 512 * (g - 1):P + 512 * g],
                                     start=(hp == 0), stop=(hp == 1))
            last.then_inc(xq_pe, 1)

        def turn_sample_probs(b):
            wait_apart(pe, tab_in, (kt_d, b * 4 + 2))
            pe.wait_ge(xq_a, b * 3 + 3)
            for n, c0 in enumerate([0] + [152 + P * m for m in range(8)]):
                pe.transpose(bank[7][:, 32 * n:32 * n + 32], xs[:, c0:c0 + P], ident[0:32, 0:32])
            pe.transpose(bank[7][0:24, 288:320], xs[:, P:P + 24], ident[0:32, 0:32]).then_inc(kt_pe, 1)

        def sample_values(b):
            pe.wait_ge(v_in, b * 112 + 112)
            wait_apart(pe, tab_in, (kt_d, b * 4 + 4))
            pe.matmul(bank[3][0:32, 0:GW], pTs[0:24, 288:320], vn[:], start=True, stop=False)
            for n in range(TILES):
                last = pe.matmul(bank[3][0:32, 0:GW], pTs[:, 32 * n:32 * n + 32], kvc[:, n, GW:2 * GW],
                                 start=False, stop=(n == TILES - 1))
            last.then_inc(sv_pe, 1)

        def turn_sample_out(b):
            wait_apart(pe, tab_in, (sn_d, b + 1))
            for hp in range(2):
                last = pe.transpose(bank[4][:, 32 * hp:32 * hp + 32], osn[:, hp * P:(hp + 1) * P], ident[0:32, 0:32])
            last.then_inc(so_pe, 1)

        def sample(b):
            st0 = Step(S_SAMPLE, (2, b))
            turn_keys(b, 0)
            turn_keys(b, 1)
            chunk(st0, FC, 0, bhi, blo)
            if above_zero(b):
                turn_sample_out(b - 1)
            turn_keys(b, 2)
            turn_keys(b, 3)
            chunk(st0, FC, 1, bhi, blo)
            turn_keys(b, 4)
            chunk(st0, FC, 2, bhi, blo)
            sample_scores(b)
            chunk(st0 + 1, KD, 0, xhi, xlo)
            chunk(st0 + 1, KD, 1, xhi, xlo)
            turn_sample_probs(b)
            chunk(st0 + 1, KD, 2, xhi, xlo)
            sample_values(b)

        pe.wait_ge(b_lo, 12)
        pe.wait_ge(pt_a, 36)
        pe.wait_ge(pt_d, 24)
        pe.wait_ge(o_a, 12)
        sample(0)
        with pe.Fori(1, NB_S) as b:
            sample(b)
        turn_sample_out(NB_S - 1)

        with pe.Fori(0, 4) as i:
            for p in range(2):
                st_ = Step(S_GATE + p, (2, i))
                chunk(st_, KD, 0, xhi, xlo)
                pe.wait_ge(ats_a, 32)
                pe.wait_ge(res_in[p], i * 32 + 32)
                pe.wait_ge(res_d, i * 6 + 3 * p)
                for t in range(TILES):
                    w = rows_of(t)
                    last = pe.transpose(bank[3 + t // 4][:, (t % 4) * P:(t % 4) * P + w], xp[p][0:w, t, :], ident[0:w, 0:w])
                    if t in (3, 7, 8):
                        last.then_inc(res_pe, 1)
                chunk(st_, KD, 1, xhi, xlo)
                chunk(st_, KD, 2, xhi, xlo)
        pe.wait_ge(at_lo, 9)
        with pe.Fori(0, 4) as i:
            for p in range(2):
                for c in range(3):
                    chunk(Step(S_MIX + p, (2, i)), 2, c, athi, atlo)
        def m_split(k):
            if k in (0, KD - 2, KD - 1):
                pe.wait_ge(m_lo, max(k + 1, KD - 2))

        for p in range(2):
            for c in range(3):
                chunk(Step(S_OUT + p), KD, c, mhi, mlo, m_split if p == 0 and c == 0 else None)
        with pe.Fori(1, 4) as i:
            for p in range(2):
                for c in range(3):
                    chunk(Step(S_OUT + p, (2, i)), KD, c, mhi, mlo)
        pe.wait_ge(sqa_p, 8)
        pe.wait_ge(ones_p, 1)
        pe.wait_ge(res_d, 24)
        for c, (t0, n) in enumerate(CH):
            pe.matmul(bank[3 + c][:, 0:n], ones[:], ssqa[:, t0:t0 + n], start=True, stop=True).then_inc(n2_pe, 1)
        pe.wait_ge(h_lo, 8)
        with pe.Fori(0, 4) as q:
            with pe.Fori(0, 4) as i:
                for p in range(2):
                    for c in range(3):
                        chunk(Step(S_MLP + p, (16, q), (2, i)), KD, c, hhi, hlo)
            with pe.Fori(0, 4) as i:
                for p in range(2):
                    for c in range(3):
                        def quarter_split(k):
                            if k == 0:
                                pe.wait_ge(f_lo, q * 24 + 21)
                            if k == KD - 1:
                                pe.wait_ge(f_lo, q * 24 + 24)
                        chunk(Step(S_MLP + 8 + p, (16, q), (2, i)), KD, c, fhi, flo,
                              quarter_split if p == 0 and c == 0 else None)
        pe.wait_ge(y_d, 96)
        pe.wait_ge(r2_d, 6)
        for t in range(TILES):
            w = rows_of(t)
            for half in range(2):
                n = 2 * t + half
                if above_zero(n - 5):
                    pe.wait_ge(yt_d, n - 5)
                for k in range(4):
                    last = pe.transpose(bank[n % 6][0:w, k * P:(k + 1) * P], x2[:, 4 * half + k, t * P:t * P + w], ident[:])
                last.then_inc(yt_pe, 1)

    @block.scalar
    def _(act):
        def split_hi(st_, nk):
            act.wait_ge(w_raw[st_.p], st_.before * 16 + 16)
            if above_zero(st_.s * 3 - 3):
                act.wait_ge(ready, st_.s * 3 - 3)
            act.activation(wh[st_.p][:, 0:nk, :], wr[st_.p][:, 0:nk, :], ACT.Copy).then_inc(w_hi, 1)

        def chunk_in(st_, c):
            act.wait_ge(ready, st_.s * 3 + (c + 1))

        act.wait_ge(bt_pe, 3)
        for g in range(NG):
            act.activation(btab[:, g * TABLE:(g + 1) * TABLE], bank[3 + g][0:12, 0:TABLE], ACT.Copy,
                           scale=1.0 / SCALE).then_inc(bt_a, 1)
        act.wait_ge(bt_a, 3)
        act.dma_start(d_bt.rearrange("h g w -> h (g w)"), btab[:]).then_inc(bt_st, 16)
        act.wait_ge(ssq_one, 1)
        for t in range(TILES):
            w = rows_of(t)
            act.wait_ge(x_in[t], 16)
            if above_zero(t):
                act.wait_ge(x_sq, t)
            act.activation(junk[0:w, :], xt[0:w, t, :], ACT.Square, accum_out=ssq[0:w, t:t + 1]).then_inc(x_sq, 1)
        act.wait_ge(rs_d, 1)
        act.activation(rst[:, 1, 0:TILES], rst[:, 0, 0:TILES], ACT.Sqrt).then_inc(rs_a, 1)
        split_hi(Step(0), KD)
        for t in range(TILES):
            w = rows_of(t)
            for half in range(2):
                n = 2 * t + half
                act.wait_ge(x_pe, n + 1)
                act.activation(xhi[:, 4 * half:4 * half + 4, t * P:t * P + w],
                               bank[3 + n % 4][:].rearrange("p (k t) -> p k t", k=4)[:, :, 0:w], ACT.Copy).then_inc(x_hi, 1)

        def token_major(kv, i, k):
            act.wait_ge(tm_pe, kv * 3 + 2)
            act.wait_ge(tm_st[k % 2], tm_before(k, i))
            act.activation(tm[k % 2][:, 4:8, :], bank[4][:].rearrange("p (i c) -> p i c", i=4), ACT.Copy).then_inc(tm_a, 1)

        def token_major_store(kv, i, k):
            p, g, cols = k % 2, k // 2, slice((k % 2) * P, (k % 2) * P + P)
            act.wait_ge(tm_a, kv + 1)
            act.wait_ge(tm_d, kv * 2 + 2)
            own = d_tm[ds(i, 1), g, :, :, cols].rearrange("o i p c -> (o i) p c")
            act.dma_start(own[0:8].rearrange("i p c -> p i c"), tm[p][:, 0:8, :]).then_inc(tm_st[p], 16)
            act.dma_start(own[8, 0:SAMP, :], tm[p][0:SAMP, 8, :]).then_inc(tm_st[p], 16)

            def part(out):
                return out.rearrange("l b n k h e -> (l b n) k (h e)")[:, ds(i, 1), cols].rearrange("n k c -> n (k c)")

            act.dma_start(part(kvs[g]), tm[p][0:SAMP, 8, :]).then_inc(tm_st[p], 16)
            out = part(kvp[g])
            if g == 0:
                act.dma_start(out, tm[p][:, 7, :]).then_inc(tm_st[p], 16)
            elif g == 1:
                act.dma_start(out.rearrange("(a r) c -> a r c", r=4), tm[p][:, 1:8:2, :]).then_inc(tm_st[p], 16)
            else:
                for q in range(2):
                    act.dma_start(out.rearrange("(m i q) c -> q m i c", i=8, q=2)[q],
                                  tm[p][64 * q:64 * q + 64, 0:8, :]).then_inc(tm_st[p], 16)

        def qkv_step(st_, d_part, k, kv, i):
            p, g = k % 2, k // 2
            split_hi(st_ + 1, KD)
            if above_zero(st_.before * 16):
                act.wait_ge(stg_st[p], st_.before * 16)
            if kv is not None:
                act.wait_ge(tm_pe, i * 18 + 3 * max(k - 1, 0))
            chunk_in(st_, 0)
            act.activation(*stage_chunk(p, g, 0), ACT.Copy).then_inc(taken[0], 1)
            if kv is not None and k:
                token_major(kv - 1, i, k - 1)
                token_major_store(kv - 1, i, k - 1)
            chunk_in(st_, 2)
            act.activation(*stage_chunk(p, g, 2), ACT.Copy).then_inc(stg_a, 1)
            act.activation(stg[p][:, SEQ:TOK], bank[2][:, SEQ - CH[2][0]:CH[2][1]], ACT.Copy).then_inc(taken[2], 1)
            act.wait_ge(stg_a, st_.s + 1)
            for c in range(3):
                act.wait_ge(taken[c], st_.s + 1)
            act.dma_start(d_part[k * P:(k + 1) * P, :], stg[p][:]).then_inc(stg_st[p], 16)

        for k in range(6):
            qkv_step(Step(k), d_T[0], k, None, 0)
        with act.Fori(0, 2) as i:
            for k in range(6):
                qkv_step(Step(6 + k, (6, i)), d_T[ds(i + 1, 1)].rearrange("o f t -> (o f) t"), k, i * 6 + k, i)
            token_major(i * 6 + 5, i, 5)
            token_major_store(i * 6 + 5, i, 5)

        def exps(g, i, p, j):
            for n in (2 * j, 2 * j + 1):
                lo = 0 if blocks(g)[n] else P
                act.wait_ge(s_d, i * 16 + (32 * g + 8 * p + n + 1))
                act.activation(pS[:, n, lo:2 * P], pS[:, n, lo:2 * P], ACT.Exp, bias=st[p][:, n:n + 1], scale=-1.0,
                               accum_out=st[p][:, 8 + n:9 + n]).then_inc(s_a, 1)

        def prompt_chunk(g, st_, f, c):
            t0, n = CH[c]
            if g == 0 and c != 1:
                for k in range(2):
                    act.wait_ge(stg_st[k], 16 * 9)
                    act.wait_ge(tm_st[k], 2 * tm_total(k))
                chunk_in(st_, c)
                act.activation(col(U, f, FC, t0, t0 + n), bank[c][:, 0:n], ACT.Copy).then_inc(taken[c], 1)
            if g == 2:
                act.wait_ge(taken[c], st_.s + 1)
                act.activation(col(bhi, f, FC, t0, t0 + n), z[:, t0:t0 + n], ACT.Copy).then_inc(b_hi, 1)

        def probs_act(g, i, p, j):
            if j == 0:
                act.wait_ge(pv_pe, i * 4 + (8 * g + 2 * p))
            act.wait_ge(pt_pe, i * 10 + (20 * g + 5 * p + j + 1))
            act.activation(*probs_copy(g, j, bank[6 + (5 * p + j) % 2]), ACT.Copy).then_inc(pt_a, 1)

        for g in range(NG):
            if g == 2:
                act.wait_ge(toe_st, 16 * 13)
                act.wait_ge(cs_ev, 1)
                act.dma_start(conv_p.rearrange("l b k c -> (l b k) c"), cst[0:2, :]).then_inc(cs_st, 16)
                act.dma_start(conv_s.rearrange("l b k c -> (l b k) c"), cst[2:18, :]).then_inc(cs_st, 16)
            with act.Fori(0, 2) as i:
                for p in range(2):
                    st_ = Step(S_PROMPT + 4 * g + p, (2, i))
                    f, u = i * 2 + p, i * 2 + (4 * g + p)
                    split_hi(st_ + 1, KD)
                    exps(g, i, p, 0)
                    exps(g, i, p, 1)
                    prompt_chunk(g, st_, f, 0)
                    exps(g, i, p, 2)
                    exps(g, i, p, 3)
                    probs_act(g, i, p, 0)
                    prompt_chunk(g, st_, f, 1)
                    probs_act(g, i, p, 2)
                    prompt_chunk(g, st_, f, 2)
                    act.wait_ge(o_st[p], i * 32 + 64 * g)
                    act.wait_ge(pv_pe, i * 4 + (8 * g + 2 * p + 2))
                    act.activation(*out_copy(g, p, 1), ACT.Copy).then_inc(o_a, 1)
                    act.wait_ge(pt_pe, i * 10 + (20 * g + 5 * p + 5))
                    act.activation(stT[p][:], bank[6 + (5 * p + 4) % 2][0:16, 0:P], ACT.Copy).then_inc(pt_a, 1)
                    act.wait_ge(o_d, u + 1)
                    act.wait_ge(o_a, u + 1)
                    act.dma_start(d_O[ds(u, 1)].rearrange("u e t -> (u e) t"), oS[p][:]).then_inc(o_st[p], 16)
                    act.wait_ge(pt_a, i * 6 + (12 * g + 3 * p + 3))
                    act.dma_start(d_st[ds(u, 1)].rearrange("u k a -> (u k) a"), stT[p][:]).then_inc(o_st[p], 16)

        def keys_act(b, j):
            act.wait_ge(kt_pe, b * 6 + (j + 1))
            if j < 4:
                c0 = P + 512 * (j % 2)
                act.activation(kTs[:, j // 2, c0:c0 + 512], bank[6][:], ACT.Copy).then_inc(kt_a, 1)
            else:
                act.activation(kTs[:, :, 0:P], bank[6][:, 0:256].rearrange("p (k c) -> p k c", k=2), ACT.Copy).then_inc(kt_a, 1)

        def coefficients_act():
            for g in range(NG):
                act.wait_ge(cf_d, 3 + g)
                act.activation(cf[:, 7 + g, :], cf[:, 7 + g, :], ACT.Exp).then_inc(cf_a, 1)
            act.wait_ge(cf_d, 14)
            for g in range(NG):
                act.dma_start(d_c[g].rearrange("h t c -> (h t) c"), cf[:, 13 + g, :]).then_inc(cf_st, 16)

        def combined_hi(n):
            act.wait_ge(cm_d, n * 3 + 3)
            act.activation(athi[:, :, ds(n * P, P)], cS[:], ACT.Copy).then_inc(at_hi, 1)

        def sample_out(b):
            act.wait_ge(so_pe, b + 1)
            for h in range(NH):
                half, hp = 64 * (h % 2), h // 2
                act.activation(ats[half:half + 64, hp, ds(b * T_S, T_S)],
                               bank[4][half:half + 64, 32 * hp + 8 * h:32 * hp + 8 * h + 8], ACT.Copy).then_inc(ats_a, 1)

        def sample(b):
            st0 = Step(S_SAMPLE, (2, b))
            split_hi(st0 + 1, KD)
            keys_act(b, 0)
            if above_zero(b):
                act.wait_ge(m_st, b * 16)
            chunk_in(st0, 0)
            act.activation(bb[:, 0:352], bank[0][:, 0:352], ACT.Copy).then_inc(taken[0], 1)
            if above_zero(b):
                sample_out(b - 1)
            keys_act(b, 2)
            keys_act(b, 4)
            chunk_in(st0, 2)
            act.activation(bb[:, 720:TOK], bank[2][:, 0:368], ACT.Copy).then_inc(taken[2], 1)
            split_hi(st0 + 2, KD)
            act.wait_ge(xq_d, b * 4 + 4)
            for k, (c0, w) in enumerate(((0, 152), (152, 512), (664, 512))):
                act.activation(xs[:, c0:c0 + w], xs[:, c0:c0 + w], ACT.Exp, bias=sm[:, 3:4], scale=-1.0,
                               accum_out=sm[:, 4 + k:5 + k]).then_inc(xq_a, 1)
            if above_zero(b):
                act.wait_ge(mb_d, b * 3)
            else:
                for p in range(2):
                    act.wait_ge(o_st[p], 32 * 6)
            for c, (t0, n) in enumerate(CH):
                chunk_in(st0 + 1, c)
                act.activation(sg[:, t0:t0 + n], bank[c][:, 0:n], ACT.Sigmoid).then_inc(taken[c], 1)
                if c == 0:
                    if above_zero(b):
                        combined_hi(b - 1)
                    else:
                        coefficients_act()
            act.wait_ge(mb_d, b * 3 + 3)
            act.dma_start(d_m[ds(b, 1)].rearrange("o p t -> (o p) t"), bb[:]).then_inc(m_st, 16)

        sample(0)
        act.wait_ge(cf_st, 48)
        with act.Fori(1, NB_S) as b:
            sample(b)

        def gate_act(i, p):
            j, st_ = i * 2 + p, Step(S_GATE + p, (2, i))
            split_hi(st_ + 1, KD)
            if isinstance(i, int) and p == 0:
                sample_out(NB_S - 1)
                combined_hi(NB_S - 1)
                act.wait_ge(ats_a, 32)
                act.activation(athi[:, :, SEQ:TOK], ats[:], ACT.Copy).then_inc(at_hi, 1)
            if p == 1:
                act.wait_ge(m_st, 16 * NB_S)
                act.wait_ge(at_lo, 9)
            for c, (t0, n) in enumerate(CH):
                chunk_in(st_, c)
                act.activation(col(sga, j, KD, t0, t0 + n), bank[c][:, 0:n], ACT.Sigmoid).then_inc(taken[c], 1)

        for p in range(2):
            gate_act(0, p)
        with act.Fori(1, 4) as i:
            for p in range(2):
                gate_act(i, p)

        def m_split_hi(j, p):
            act.wait_ge(mt_p, j + 1)
            act.activation(col(mhi, j, KD, 0, TOK), mt[p][:], ACT.Copy).then_inc(m_hi, 1)

        split_hi(Step(S_MIX + 1), 2)
        with act.Fori(0, 3) as i:
            for p in range(2):
                split_hi(Step(S_MIX + 2 + p, (2, i)), 2)
                m_split_hi(i * 2 + p, p)
        split_hi(Step(S_OUT), KD)
        for j in (6, 7):
            m_split_hi(j, j % 2)
        with act.Fori(0, 4) as i:
            for p in range(2):
                j, st_ = i * 2 + p, Step(S_OUT + p, (2, i))
                split_hi(st_ + 1, KD)
                for c in range(3):
                    act.wait_ge(taken[c], st_.s + 1)
                act.activation(col(hhi, j, KD, 0, TOK), col(x2, j, KD, 0, TOK), ACT.Copy, scale=g2c[:, ds(j, 1)]).then_inc(h_hi, 1)
                wait_apart(act, tab_in, (sqa_p, j))
                act.activation(sq2[:], col(x2, j, KD, 0, TOK), ACT.Square).then_inc(sq_a, 1)
        act.wait_ge(n2_pe, 3)

        def up_act(q, i, p):
            st_ = Step(S_MLP + p, (16, q), (2, i))
            split_hi(st_ + 1, KD)
            for c, (t0, n) in enumerate(CH):
                e = q * 24 + (i * 6 + (3 * p + c))
                r = rel[(p + c) % 2]
                chunk_in(st_, c)
                act.wait_ge(f_lo, q * 24 + (i * 6 + max(3 * p + c - 1, 0)))
                act.activation(r[:, 0:n], bank[c][:, 0:n], ACT.Relu).then_inc(f_rel, 1)
                act.wait_ge(taken[c], st_.s + 1)
                act.activation(col(fhi, i * 2 + p, KD, t0, t0 + n), r[:, 0:n], ACT.Copy).then_inc(f_hi, 1)

        def down_act(q, i, p):
            split_hi(Step(S_MLP + 8 + p, (16, q), (2, i)) + 1, KD)

        with act.Fori(0, 3) as q:
            with act.Fori(0, 4) as i:
                for p in range(2):
                    up_act(q, i, p)
            with act.Fori(0, 4) as i:
                for p in range(2):
                    down_act(q, i, p)
        with act.Fori(0, 4) as i:
            for p in range(2):
                up_act(3, i, p)
        with act.Fori(0, 3) as i:
            for p in range(2):
                down_act(3, i, p)
        down_act(3, 3, 0)
        for t in range(TILES):
            w = rows_of(t)
            for half in range(2):
                n = 2 * t + half
                act.wait_ge(yt_pe, n + 1)
                if above_zero(n - 1):
                    act.wait_ge(yt_a, n - 1)
                act.activation(yj[0:w, half, :], bank[n % 6][0:w, :], ACT.Square,
                               accum_out=rst[0:w, 2 + half, t:t + 1]).then_inc(yt_a, 1)
            act.wait_ge(yn_d, 6 * t + 2)
            act.activation(rst[0:w, 1, t:t + 1], rst[0:w, 0, t:t + 1], ACT.Sqrt).then_inc(yr_a, 1)

    @block.vector
    def _(dve):
        f32 = lambda ap: ap.bitcast(F32)

        def split_lo(st_, nk):
            dve.wait_ge(w_hi, st_.s + 1)
            dve.tensor_tensor(wl[st_.p][:, 0:nk, :], wr[st_.p][:, 0:nk, :], f32(wh[st_.p][:, 0:nk, :]),
                              ALU.subtract).then_inc(w_lo, 1)

        def chunk_in(st_, c):
            dve.wait_ge(ready, st_.s * 3 + (c + 1))

        def rstd(sem_d, base, sem_a, roots, sl):
            v, root, r, t, y = (rst[sl[0], k, sl[1]] for k in (0, 1, 4, 2, 3))
            dve.wait_ge(sem_a, roots)
            dve.reciprocal(r, root).then_inc(sem_d, 1)
            dve.wait_ge(sem_d, base + 1)
            dve.scalar_tensor_tensor(t, r, 1.0, r, ALU.mult, ALU.mult).then_inc(sem_d, 1)
            dve.wait_ge(sem_d, base + 2)
            dve.scalar_tensor_tensor(y, t, -0.5, v, ALU.mult, ALU.mult).then_inc(sem_d, 1)
            dve.wait_ge(sem_d, base + 3)
            dve.scalar_tensor_tensor(r, y, 1.5, r, ALU.add, ALU.mult).then_inc(sem_d, 1)
            dve.wait_ge(sem_d, base + 4)

        dve.wait_ge(bt_pe, 4)
        dve.tensor_copy(cT[:], bank[6][:, 0:80]).then_inc(const_d, 1)
        dve.tensor_copy(g2c[:], bank[6][:, 80:88]).then_inc(const_d, 1)
        dve.wait_ge(x_sq, TILES)
        dve.tensor_scalar(rst[:, 0, 0:TILES], ssq[:, 0:TILES], 1.0 / D, EPS, ALU.mult, ALU.add).then_inc(rs_d, 1)
        rstd(rs_d, 1, rs_a, 1, (slice(None), slice(0, TILES)))
        dve.wait_ge(gb_in, 16)
        for t in range(TILES + 1):
            if t < TILES:
                w = rows_of(t)
                dve.scalar_tensor_tensor(xt[0:w, t, :], xt[0:w, t, :], rst[0:w, 4, t:t + 1], gb[0:w, :],
                                         ALU.mult, ALU.mult).then_inc(x_scaled, 1)
            if t:
                w = rows_of(t - 1)
                for half in range(2):
                    n = 2 * (t - 1) + half
                    cut = (slice(None), slice(4 * half, 4 * half + 4), slice((t - 1) * P, (t - 1) * P + w))
                    dve.wait_ge(x_hi, n + 1)
                    dve.tensor_tensor(xlo[cut], bank[3 + n % 4][:].rearrange("p (k t) -> p k t", k=4)[:, :, 0:w],
                                      f32(xhi[cut]), ALU.subtract).then_inc(x_lo, 1)
            if t == 1:
                split_lo(Step(0), KD)

        def token_major(kv, i, k, grp):
            dve.wait_ge(tm_pe, kv * 3 + (grp + 1))
            dve.wait_ge(tm_st[k % 2], tm_before(k, i))
            if grp == 0:
                dve.tensor_copy(tm[k % 2][:, 0:4, :], bank[3][:].rearrange("p (i c) -> p i c", i=4)).then_inc(tm_d, 1)
            else:
                dve.tensor_copy(tm[k % 2][0:SAMP, 8, :], bank[5][0:SAMP, 0:P]).then_inc(tm_d, 1)

        def qkv_step(st_, k, kv, i):
            p, g = k % 2, k // 2
            split_lo(st_ + 1, KD)
            if kv is not None and k:
                token_major(kv - 1, i, k - 1, 0)
            if above_zero(st_.before * 16):
                dve.wait_ge(stg_st[p], st_.before * 16)
            if kv is not None:
                dve.wait_ge(tm_pe, i * 18 + 3 * max(k - 1, 0))
            chunk_in(st_, 1)
            dve.tensor_copy(*stage_chunk(p, g, 1)).then_inc(taken[1], 1)
            if kv is not None and k:
                token_major(kv - 1, i, k - 1, 2)

        for k in range(6):
            qkv_step(Step(k), k, None, 0)
        with dve.Fori(0, 2) as i:
            for k in range(6):
                qkv_step(Step(6 + k, (6, i)), k, i * 6 + k, i)
            token_major(i * 6 + 5, i, 5, 0)
            token_major(i * 6 + 5, i, 5, 2)

        def bias_scores(g, i, p, j):
            if j == 0:
                dve.wait_ge(u_in[p], i * 64 + 64 * (2 * g + 1))
                dve.wait_ge(pt_pe, i * 10 + (20 * g + 5 * p))
            wait_apart(dve, tab_in, (s_pe, i * 8 + (16 * g + 4 * p + j + 1)))
            for n in (2 * j, 2 * j + 1):
                lo = 0 if blocks(g)[n] else P
                c0 = (n % 2) * 256
                dve.tensor_tensor_reduce(pS[:, n, lo:2 * P], bank[3 + j % 2][:, c0 + lo:c0 + 256], bU[p][:, lo:2 * P],
                                         -SCALE, HUGE, ALU.add, ALU.min, st[p][:, n:n + 1]).then_inc(s_d, 1)

        def z_terms(f, i):
            w = lambda k: cT[:, ds(f * 20 + (16 + k), 1)]
            last = lambda n: dve.wait_ge(z_d, f * 7 + n)
            dve.wait_ge(b_hi, f * 3)
            dve.wait_ge(b_lo, f * 3)
            dve.tensor_scalar(z[:], col(U, f, FC, 0, TOK), w(2), w(3), ALU.mult, ALU.add).then_inc(z_d, 1)
            dve.tensor_copy(us[:, :, 0:2], cT[:, ds(f * 20, 16)].rearrange("p (b k) -> p b k", k=2)).then_inc(z_d, 1)
            dve.tensor_copy(us[:, :, 2:2 + T_S], col(U, f, FC, SEQ, TOK).rearrange("p (b t) -> p b t", t=T_S)).then_inc(z_d, 1)
            zs = z[:, SEQ:TOK].rearrange("p (b t) -> p b t", t=T_S)
            for k in (1, 0):
                last(3 if k else 5)
                dve.scalar_tensor_tensor(z[:, 2 - k:SEQ], col(U, f, FC, 0, SEQ - 2 + k), w(k), z[:, 2 - k:SEQ],
                                         ALU.mult, ALU.add).then_inc(z_d, 1)
                dve.scalar_tensor_tensor(zs, us[:, :, k:k + T_S], w(k), zs, ALU.mult, ALU.add).then_inc(z_d, 1)
            last(7)

        def prompt_chunk(g, st_, f, c):
            t0, n = CH[c]
            if g == 0 and c == 1:
                for k in range(2):
                    dve.wait_ge(stg_st[k], 16 * 9)
                    dve.wait_ge(tm_st[k], 2 * tm_total(k))
                chunk_in(st_, c)
                dve.tensor_copy(col(U, f, FC, t0, t0 + n), bank[c][:, 0:n]).then_inc(taken[c], 1)
            if g == 1:
                chunk_in(st_, c)
                u = col(U, f, FC, t0, t0 + n)
                dve.tensor_tensor(u, bank[c][:, 0:n], u, ALU.mult).then_inc(taken[c], 1)
            if g == 2:
                chunk_in(st_, c)
                dve.tensor_tensor(z[:, t0:t0 + n], bank[c][:, 0:n], z[:, t0:t0 + n], ALU.mult).then_inc(taken[c], 1)
                dve.wait_ge(b_hi, f * 3 + (c + 1))
                dve.tensor_tensor(col(blo, f, FC, t0, t0 + n), z[:, t0:t0 + n], f32(col(bhi, f, FC, t0, t0 + n)),
                                  ALU.subtract).then_inc(b_lo, 1)

        def probs_dve(g, i, p, j):
            dve.wait_ge(pt_pe, i * 10 + (20 * g + 5 * p + j + 1))
            dve.wait_ge(pt_a, i * 6 + (12 * g + 3 * p + 1))
            dve.tensor_copy(*probs_copy(g, j, bank[6 + (5 * p + j) % 2])).then_inc(pt_d, 1)

        for g in range(NG):
            if g:
                for c in range(3):
                    dve.wait_ge(taken[c], S_PROMPT + 4 * g)
            if g == 2:
                dve.tensor_copy(csb[:, :, 0:2], U[:, :, SEQ - 2:SEQ]).then_inc(cs_d, 1)
                dve.tensor_copy(csb[:, :, 2:18].rearrange("p f (b k) -> p f b k", k=2),
                                U[:, :, SEQ:TOK].rearrange("p f (b t) -> p f b t", t=T_S)[:, :, :, T_S - 2:T_S]).then_inc(cs_d, 1)
                dve.wait_ge(cs_pe, 1)
                dve.tensor_copy(cst[:], bank[3][0:18, :]).then_inc(cs_ev, 1)
            with dve.Fori(0, 2) as i:
                for p in range(2):
                    st_ = Step(S_PROMPT + 4 * g + p, (2, i))
                    f = i * 2 + p
                    split_lo(st_ + 1, KD)
                    bias_scores(g, i, p, 0)
                    bias_scores(g, i, p, 1)
                    if g == 2:
                        z_terms(f, i)
                    prompt_chunk(g, st_, f, 0)
                    bias_scores(g, i, p, 2)
                    bias_scores(g, i, p, 3)
                    probs_dve(g, i, p, 1)
                    prompt_chunk(g, st_, f, 1)
                    probs_dve(g, i, p, 3)
                    dve.wait_ge(o_st[p], i * 32 + 64 * g)
                    dve.wait_ge(pv_pe, i * 4 + (8 * g + 2 * p + 1))
                    dve.tensor_copy(*out_copy(g, p, 0)).then_inc(o_d, 1)
                    prompt_chunk(g, st_, f, 2)

        def by_token(tile, g):
            dil = GROUPS[g][1]
            return tile if dil == 1 else tile.rearrange("p (r m) -> p m r", r=dil)

        def like(tile, g):
            dil = GROUPS[g][1]
            return tile if dil == 1 else tile.rearrange("p (m r) -> p m r", r=dil)

        T = lambda k: cf[:, k, :]

        def coefficients_dve():
            dve.wait_ge(cf_in, 16 * 18)
            dve.tensor_tensor(like(T(6), 1), like(T(0), 1), by_token(T(1), 1), ALU.min).then_inc(cf_d, 1)
            dve.wait_ge(cf_d, 1)
            dve.tensor_tensor(like(T(6), 2), like(T(6), 2), by_token(T(2), 2), ALU.min).then_inc(cf_d, 1)
            dve.wait_ge(cf_d, 2)
            for g in range(NG):
                dve.tensor_tensor(like(T(7 + g), g), like(T(6), g), by_token(T(g), g), ALU.subtract).then_inc(cf_d, 1)
            for g in range(NG):
                dve.wait_ge(cf_a, g + 1)
                dve.tensor_tensor(like(T(10 + g), g), like(T(7 + g), g), by_token(T(3 + g), g), ALU.mult).then_inc(cf_d, 1)
            dve.wait_ge(cf_d, 8)
            dve.tensor_tensor(T(16), T(10), T(11), ALU.add).then_inc(cf_d, 1)
            dve.wait_ge(cf_d, 9)
            dve.tensor_tensor(T(17), T(16), T(12), ALU.add).then_inc(cf_d, 1)
            dve.wait_ge(cf_d, 10)
            dve.reciprocal(T(16), T(17)).then_inc(cf_d, 1)
            dve.wait_ge(cf_d, 11)
            for g in range(NG):
                dve.tensor_tensor(T(13 + g), T(7 + g), T(16), ALU.mult).then_inc(cf_d, 1)

        def keys_dve(b, j):
            dve.wait_ge(kt_pe, b * 6 + (j + 1))
            dve.tensor_copy(kTs[:, j // 2, P + 512:P + 1024], bank[7][:]).then_inc(kt_d, 1)

        def combined(n):
            dve.wait_ge(cm_in, n * 96 + 96)
            dve.tensor_tensor(cO[:], cO[:], cC[:], ALU.mult).then_inc(cm_d, 1)
            dve.wait_ge(cm_d, n * 3 + 1)
            if above_zero(n):
                dve.wait_ge(at_lo, n)
            dve.tensor_tensor(cS[:], cO[:, :, 0, :], cO[:, :, 1, :], ALU.add).then_inc(cm_d, 1)
            dve.wait_ge(cm_d, n * 3 + 2)
            dve.tensor_tensor(cS[:], cS[:], cO[:, :, 2, :], ALU.add).then_inc(cm_d, 1)

        def combined_lo(n):
            dve.wait_ge(at_hi, n + 1)
            dve.tensor_tensor(atlo[:, :, ds(n * P, P)], cS[:], f32(athi[:, :, ds(n * P, P)]), ALU.subtract).then_inc(at_lo, 1)

        def gated(b, st_, c):
            t0, n = CH[c]
            dve.wait_ge(taken[c], st_.s + 1)
            dve.tensor_tensor(bb[:, t0:t0 + n], bb[:, t0:t0 + n], sg[:, t0:t0 + n], ALU.mult).then_inc(mb_d, 1)

        def sample(b):
            st0 = Step(S_SAMPLE, (2, b))
            split_lo(st0 + 1, KD)
            keys_dve(b, 1)
            keys_dve(b, 3)
            if above_zero(b):
                dve.wait_ge(m_st, b * 16)
            chunk_in(st0, 1)
            dve.tensor_copy(bb[:, 352:720], bank[1][:, 0:368]).then_inc(taken[1], 1)
            wait_apart(dve, tab_in, (xq_pe, b + 1), (kt_pe, b * 6))
            for k, (c0, w, src) in enumerate(((0, 152, 3), (152, 512, 4), (664, 512, 5))):
                dve.tensor_tensor_reduce(xs[:, c0:c0 + w], bank[src][0:32, 0:w], bias_s[:, c0:c0 + w],
                                         -SCALE, HUGE, ALU.add, ALU.min, sm[:, k:k + 1]).then_inc(xq_d, 1)
            dve.wait_ge(xq_d, b * 4 + 3)
            dve.tensor_reduce(sm[:, 3:4], sm[:, 0:3], AX_X, ALU.min).then_inc(xq_d, 1)
            split_lo(st0 + 2, KD)
            if above_zero(b):
                combined(b - 1)
            gated(b, st0 + 1, 0)
            dve.wait_ge(xq_a, b * 3 + 3)
            dve.tensor_reduce(sm[:, 7:8], sm[:, 4:7], AX_X, ALU.add).then_inc(rl_d, 1)
            dve.wait_ge(rl_d, b * 2 + 1)
            dve.reciprocal(sm[:, 8:9], sm[:, 7:8]).then_inc(rl_d, 1)
            if above_zero(b):
                combined_lo(b - 1)
            else:
                coefficients_dve()
            gated(b, st0 + 1, 1)
            if above_zero(b):
                dve.wait_ge(sv_pe, b)
            dve.wait_ge(kt_pe, b * 6 + 6)
            dve.tensor_copy(pTs[:, 0:288], bank[7][:, 0:288]).then_inc(kt_d, 1)
            dve.tensor_copy(pTs[0:24, 288:320], bank[7][0:24, 288:320]).then_inc(kt_d, 1)
            gated(b, st0 + 1, 2)
            dve.wait_ge(sv_pe, b + 1)
            if above_zero(b):
                dve.wait_ge(so_pe, b)
            dve.wait_ge(rl_d, b * 2 + 2)
            dve.tensor_scalar(osn[:], bank[3][0:32, 0:GW], sm[:, 8:9], None, ALU.mult).then_inc(sn_d, 1)

        dve.wait_ge(sb_in, 16 * 33)
        sample(0)
        dve.wait_ge(cf_st, 48)
        with dve.Fori(1, NB_S) as b:
            sample(b)

        def gate_dve(i, p):
            j = i * 2 + p
            split_lo(Step(S_GATE + 1 + p, (2, i)), KD)
            if isinstance(i, int) and p == 0:
                combined(NB_S - 1)
                combined_lo(NB_S - 1)
                dve.wait_ge(at_hi, 9)
                dve.tensor_tensor(atlo[:, :, SEQ:TOK], ats[:], f32(athi[:, :, SEQ:TOK]), ALU.subtract).then_inc(at_lo, 1)
            for k in range(3):
                dve.wait_ge(res_pe, j * 3 + (k + 1))
                n = 512 if k < 2 else SAMP
                dve.tensor_copy(col(x2, j, KD, 512 * k, 512 * k + n), bank[3 + k][:, 0:n]).then_inc(res_d, 1)

        for p in range(2):
            gate_dve(0, p)
        with dve.Fori(1, 4) as i:
            for p in range(2):
                gate_dve(i, p)

        def mixed(st_, nk_next, j, p):
            split_lo(st_ + 1, nk_next)
            if above_zero(j - 1):
                dve.wait_ge(m_lo, j - 1)
            for c, (t0, n) in enumerate(CH):
                chunk_in(st_, c)
                dve.tensor_tensor(mt[p][:, t0:t0 + n], bank[c][:, 0:n], col(sga, j, KD, t0, t0 + n), ALU.mult).then_inc(taken[c], 1)

        def m_split_lo(j, p):
            dve.wait_ge(m_hi, j + 1)
            dve.tensor_tensor(col(mlo, j, KD, 0, TOK), mt[p][:], f32(col(mhi, j, KD, 0, TOK)), ALU.subtract).then_inc(m_lo, 1)

        mixed(Step(S_MIX), 2, 0, 0)
        with dve.Fori(0, 3) as i:
            mixed(Step(S_MIX + 1, (2, i)), 2, i * 2 + 1, 1)
            m_split_lo(i * 2, 0)
            mixed(Step(S_MIX + 2, (2, i)), 2, i * 2 + 2, 0)
            m_split_lo(i * 2 + 1, 1)
        mixed(Step(S_MIX + 7), KD, 7, 1)
        for j in (6, 7):
            m_split_lo(j, j % 2)
        dve.wait_ge(res_d, 24)
        with dve.Fori(0, 4) as i:
            for p in range(2):
                j, st_ = i * 2 + p, Step(S_OUT + p, (2, i))
                split_lo(st_ + 1, KD)
                for c, (t0, n) in enumerate(CH):
                    chunk_in(st_, c)
                    x = col(x2, j, KD, t0, t0 + n)
                    dve.tensor_tensor(x, bank[c][:, 0:n], x, ALU.add).then_inc(taken[c], 1)
                dve.wait_ge(h_hi, j + 1)
                dve.scalar_tensor_tensor(col(hlo, j, KD, 0, TOK), col(x2, j, KD, 0, TOK), g2c[:, ds(j, 1)],
                                         f32(col(hhi, j, KD, 0, TOK)), ALU.mult, ALU.subtract).then_inc(h_lo, 1)
        for c, (t0, n) in enumerate(CH):
            dve.wait_ge(n2_pe, c + 1)
            dve.tensor_scalar(r2b[:, t0:t0 + n], bank[3 + c][:, 0:n], 1.0 / D, EPS, ALU.mult, ALU.add).then_inc(r2_d, 1)
            dve.wait_ge(r2_d, 2 * c + 1)
            dve.reciprocal(r2b[:, t0:t0 + n], r2b[:, t0:t0 + n]).then_inc(r2_d, 1)

        dve.wait_ge(r2_d, 6)

        def up_dve(q, i, p):
            st_ = Step(S_MLP + p, (16, q), (2, i))
            split_lo(st_ + 1, KD)
            for c, (t0, n) in enumerate(CH):
                e = q * 24 + (i * 6 + (3 * p + c + 1))
                r = rel[(p + c) % 2]
                dve.wait_ge(f_rel, e)
                dve.tensor_tensor(r[:, 0:n], bank[c][:, 0:n], r[:, 0:n], ALU.mult).then_inc(taken[c], 1)
                dve.wait_ge(f_hi, e)
                dve.tensor_tensor(col(flo, i * 2 + p, KD, t0, t0 + n), r[:, 0:n], f32(col(fhi, i * 2 + p, KD, t0, t0 + n)),
                                  ALU.subtract).then_inc(f_lo, 1)

        def down_dve(q, i, p, split=True):
            st_ = Step(S_MLP + 8 + p, (16, q), (2, i))
            if split:
                split_lo(st_ + 1, KD)
            for c, (t0, n) in enumerate(CH):
                e = q * 24 + (i * 6 + (3 * p + c))
                chunk_in(st_, c)
                dve.wait_ge(y_d, e)
                dve.tensor_tensor(acc[:, 0:n], bank[c][:, 0:n], r2b[:, t0:t0 + n], ALU.mult).then_inc(taken[c], 1)
                dve.wait_ge(taken[c], st_.s + 1)
                x = col(x2, i * 2 + p, KD, t0, t0 + n)
                dve.tensor_tensor(x, acc[:, 0:n], x, ALU.add).then_inc(y_d, 1)

        with dve.Fori(0, 3) as q:
            with dve.Fori(0, 4) as i:
                for p in range(2):
                    up_dve(q, i, p)
            with dve.Fori(0, 4) as i:
                for p in range(2):
                    down_dve(q, i, p)
        with dve.Fori(0, 4) as i:
            for p in range(2):
                up_dve(3, i, p)
        with dve.Fori(0, 3) as i:
            for p in range(2):
                down_dve(3, i, p)
        down_dve(3, 3, 0)
        down_dve(3, 3, 1, split=False)

        dve.wait_ge(gf_in, 16)
        for t in range(TILES):
            w = rows_of(t)
            dve.wait_ge(yt_a, 2 * t + 2)
            dve.tensor_tensor(rst[0:w, 0, t:t + 1], rst[0:w, 2, t:t + 1], rst[0:w, 3, t:t + 1], ALU.add).then_inc(yn_d, 1)
            dve.wait_ge(yn_d, 6 * t + 1)
            dve.tensor_scalar(rst[0:w, 0, t:t + 1], rst[0:w, 0, t:t + 1], 1.0 / D, EPS, ALU.mult, ALU.add).then_inc(yn_d, 1)
            rstd(yn_d, 6 * t + 2, yr_a, t + 1, (slice(0, w), slice(t, t + 1)))
            if above_zero(16 * (t // 3)):
                dve.wait_ge(y_st[t % 3], 16 * (t // 3))
            for half in range(2):
                cut = slice(512 * half, 512 * half + 512)
                dve.scalar_tensor_tensor(yt[t % 3][0:w, cut], bank[(2 * t + half) % 6][0:w, :], rst[0:w, 4, t:t + 1],
                                         gf[0:w, cut], ALU.mult, ALU.mult).then_inc(yt_d, 1)

    @block.gpsimd
    def _(pool):
        pool.memset(relb[N_BUCKETS:N_BUCKETS + 1, :], 1.0).then_inc(relb_one, 1)
        pool.wait_ge(relb_one, 1)
        pool.memset(ssq[:], 1.0).then_inc(ssq_one, 1)
        pool.wait_ge(ssq_one, 1)
        pool.memset(toe2[:], NEG / SCALE).then_inc(toe_neg, 1)
        pool.wait_ge(toe_neg, 1)
        pool.memset(bias_s[:], NEG / SCALE).then_inc(sbias_neg, 1)
        pool.wait_ge(pv_pe, 24)
        pool.wait_ge(sbias_neg, 1)
        pool.memset(qbd[:], 0.0).then_inc(q_zero, 1)
        with pool.Fori(0, 4) as i:
            for p in range(2):
                for c in range(3):
                    pool.wait_ge(taken[c], Step(S_MIX + 1 + p, (2, i)).s)
                pool.wait_ge(mix_in[p], i * 16 + 16)
                pool.tensor_tensor(mt[p][:], mt[p][:], ml[p][:], ALU.add).then_inc(mt_p, 1)
                pool.wait_ge(mt_p, i * 2 + (p + 1))
        pool.wait_ge(at_lo, 9)
        pool.wait_ge(q_zero, 1)
        pool.memset(ones[:], 1.0).then_inc(ones_p, 1)
        pool.wait_ge(ones_p, 1)
        pool.memset(ssqa[:], 0.0).then_inc(ones_p, 1)
        pool.wait_ge(ones_p, 2)
        with pool.Fori(0, KD) as j:
            pool.wait_ge(sq_a, j + 1)
            pool.tensor_tensor(ssqa[:], ssqa[:], sq2[:], ALU.add).then_inc(sqa_p, 1)
            pool.wait_ge(sqa_p, j + 1)

    es.close()


_INS = ["x_prompt", "x_sample", "cache_kv_g0", "cache_kv_g1", "cache_kv_g2", "state_conv", "w_in", "w_att_out",
        "w_conv_out", "w_o", "conv_w", "conv_b", "rel_bias", "norm_mix", "norm_mlp", "w_ff1", "w_ff2", "norm_final"]
_OUTS = [(1, SEQ, D), (NB_S, T_S, D), (1, 1, 128, 2, 4, 64), (1, 1, 512, 2, 4, 64), (1, 1, 1024, 2, 4, 64),
         (1, 1, 2, CONV_W), (1, NB_S, T_S, 2, 4, 64), (1, NB_S, T_S, 2, 4, 64), (1, NB_S, T_S, 2, 4, 64),
         (1, NB_S, 2, CONV_W)]


def kernel(**inputs):
    import numpy as _np
    import concourse.bacc as _bacc
    from concourse import mybir as _mybir
    from concourse.bass_utils import run_bass_kernel_spmd as _run

    nc = _bacc.Bacc("TRN2", target_bir_lowering=False, num_devices=1)
    arrays, args = {}, {}
    given = {name: _np.ascontiguousarray(inputs[name]) for name in _INS}
    given["selector"] = bias_selector()
    given["identity"] = _np.eye(P, dtype=_np.float32)
    for name, a in given.items():
        arrays[f"in_{name}_dram"] = a
        args[name] = nc.dram_tensor(f"in_{name}_dram", a.shape, _mybir.dt.from_np(a.dtype), kind="ExternalInput").ap()
    o = [nc.dram_tensor(f"out_{i}_dram", shape, F32, kind="ExternalOutput").ap() for i, shape in enumerate(_OUTS)]
    build(nc, args["x_prompt"], args["x_sample"], [args[f"cache_kv_g{g}"] for g in range(NG)], args["state_conv"],
          args["w_in"][0], args["w_att_out"][0], args["w_conv_out"][0], args["w_o"][0], args["conv_w"], args["conv_b"],
          args["rel_bias"], args["norm_mix"], args["norm_mlp"], args["w_ff1"][0], args["w_ff2"][0], args["norm_final"],
          args["selector"], args["identity"], o[0], o[1], o[2:5], o[5], o[6:9], o[9])
    r = _run(nc, [arrays], core_ids=[0])
    return tuple(r.results[0][f"out_{i}_dram"] for i in range(len(_OUTS)))
```
